# Optimizing a Trainium2 kernel written in Bass

```python
import math
import jax, jax.numpy as jnp
from jax import lax
import numpy as np

D_MODEL = 1024
BATCH = 1
SEQ = 128
DEPTH = 2
DEC_BATCH = 1
DEC_SEQ = 128
PAST_LEN = 128

GRID_W = 64
MIX_WIDTH = D_MODEL
DA_HEADS = 4
DA_QK = 64
DA_V = 2 * DA_QK
DA_WIDTH = DA_HEADS * DA_V
NA_HEADS = 4
NA_DIM = 64
NA_WIDTH = NA_HEADS * NA_DIM
NA_ROWS = 8
NA_COLS = 16
NA_QBLOCK = 16
NA_KBAND = 2 * NA_COLS
POOL_WINDOWS = (2, 4, 8, 16)
POOL_CH = 64
POOL_WIDTH = len(POOL_WINDOWS) * POOL_CH
IN_COLS = 3 * DA_WIDTH + 3 * NA_WIDTH + POOL_WIDTH
ROPE_THETA = 10000.0
Q_BLOCK = 128
N_EXPERTS = 64
TOP_K = 8
N_GROUPS = 8
TOPK_GROUPS = 4
EXPERT_DIM = 256
SHARED_DIM = 256
ROUTED_SCALE = 2.5
EPS = 1e-6
NEG = -1e30

kernel_name = 'hybrid_diffattn_natten_pool_moe_prefix_step'

def rmsnorm(x, g):
    xf = x.astype(jnp.float32)
    y = xf * lax.rsqrt(jnp.mean(xf * xf, axis=-1, keepdims=True) + EPS)
    return (y * g.astype(jnp.float32)).astype(x.dtype)

def modulation(cvec, w, b):
    m = jax.nn.silu(cvec) @ w + b
    return jnp.split(m[:, None, :], 6, axis=-1)

def adaln(h, shift, scale):
    return h * (1 + scale) + shift

def axial_rope(x):
    b, n, h, dim = x.shape
    nf = dim // 4
    t = jnp.arange(n, dtype=jnp.int32)
    pos = jnp.stack([t // GRID_W, t % GRID_W], axis=-1).astype(jnp.float32)
    inv = jnp.power(ROPE_THETA, -jnp.arange(nf, dtype=jnp.float32) / nf)
    ang = pos[:, :, None] * inv
    cos = jnp.cos(ang)[None, :, None]
    sin = jnp.sin(ang)[None, :, None]
    xr = x.astype(jnp.float32).reshape(b, n, h, 2, 2, nf)
    x1, x2 = xr[..., 0, :], xr[..., 1, :]
    out = jnp.stack([x1 * cos - x2 * sin, x2 * cos + x1 * sin], axis=-2)
    return out.reshape(b, n, h, dim).astype(x.dtype)

def _query_blocks(nq):
    blk = Q_BLOCK if nq % Q_BLOCK == 0 else nq
    return blk, nq // blk

def diff_attention(q, k, v, lam):
    b, nq, h, _, dq = q.shape
    blk, nblk = _query_blocks(nq)
    qs = jnp.moveaxis(q.reshape(b, nblk, blk, h, 2, dq), 1, 0)
    scale = dq ** -0.5

    def one_block(qi):
        s = jnp.einsum('bqhmd,bkhmd->bhmqk', qi, k).astype(jnp.float32) * scale
        p = jax.nn.softmax(s, axis=-1)
        w = p[:, :, 0] - lam * p[:, :, 1]
        return jnp.einsum('bhqk,bkhd->bqhd', w.astype(v.dtype), v)

    o = lax.map(one_block, qs)
    return jnp.moveaxis(o, 0, 1).reshape(b, nq, h, v.shape[-1])

def dense_attention(q, k, v):
    b, nq, h, d = q.shape
    blk, nblk = _query_blocks(nq)
    qs = jnp.moveaxis(q.reshape(b, nblk, blk, h, d), 1, 0)
    scale = d ** -0.5

    def one_block(qi):
        s = jnp.einsum('bqhd,bkhd->bhqk', qi, k).astype(jnp.float32) * scale
        p = jax.nn.softmax(s, axis=-1)
        return jnp.einsum('bhqk,bkhd->bqhd', p.astype(v.dtype), v)

    o = lax.map(one_block, qs)
    return jnp.moveaxis(o, 0, 1).reshape(b, nq, h, v.shape[-1])

def neighbourhood_attention(q, k, v, k_ctx, v_ctx, bias_table):
    b, n, h, d = q.shape
    rows = n // GRID_W
    kr = min(NA_ROWS, rows)
    ncb = GRID_W // NA_QBLOCK
    r = jnp.arange(rows)
    row_start = jnp.clip(r - kr // 2, 0, rows - kr)
    row_idx = row_start[:, None] + jnp.arange(kr)[None, :]
    cpos = jnp.arange(GRID_W)
    col_start = jnp.clip(cpos - NA_COLS // 2, 0, GRID_W - NA_COLS)
    band_start = jnp.clip(col_start[::NA_QBLOCK], 0, GRID_W - NA_KBAND)
    col_idx = band_start[:, None] + jnp.arange(NA_KBAND)[None, :]
    kg = k.reshape(b, rows, GRID_W, h, d)
    vg = v.reshape(b, rows, GRID_W, h, d)
    ridx = row_idx[:, None, :, None]
    cidx = col_idx[None, :, None, :]
    k_blk = kg[:, ridx, cidx]
    v_blk = vg[:, ridx, cidx]
    qg = q.reshape(b, rows, ncb, NA_QBLOCK, h, d)
    scale = d ** -0.5
    s_loc = jnp.einsum('brnqhd,brnikhd->bhrnqik', qg, k_blk).astype(jnp.float32) * scale
    qcol = cpos.reshape(ncb, NA_QBLOCK)
    qcs = col_start[qcol]
    kcol = col_idx[:, None, :]
    valid = (kcol >= qcs[:, :, None]) & (kcol < qcs[:, :, None] + NA_COLS)
    off_r = (row_idx - r[:, None] + NA_ROWS - 1)[:, None, None, :, None]
    off_c = jnp.clip(kcol - qcol[:, :, None] + NA_COLS - 1, 0, 2 * NA_COLS - 2)[None, :, :, None, :]
    bias = bias_table.astype(jnp.float32)[:, off_r, off_c]
    s_loc = jnp.where(valid[None, None, None, :, :, None, :], s_loc + bias[None], NEG)
    s_loc = s_loc.reshape(b, h, rows, ncb, NA_QBLOCK, kr * NA_KBAND)
    s_ctx = jnp.einsum('brnqhd,blhd->bhrnql', qg, k_ctx).astype(jnp.float32) * scale
    p = jax.nn.softmax(jnp.concatenate([s_loc, s_ctx], axis=-1), axis=-1)
    p_loc = p[..., :kr * NA_KBAND].reshape(b, h, rows, ncb, NA_QBLOCK, kr, NA_KBAND)
    p_ctx = p[..., kr * NA_KBAND:]
    o = jnp.einsum('bhrnqik,brnikhd->brnqhd', p_loc.astype(v.dtype), v_blk)
    o = o + jnp.einsum('bhrnql,blhd->brnqhd', p_ctx.astype(v.dtype), v_ctx)
    return o.reshape(b, n, h, d)

def multiscale_pool(u, w_pool, scale):
    b, n, _ = u.shape
    uf = u.astype(jnp.float32)
    csum = jnp.concatenate([jnp.zeros((b, 1, POOL_WIDTH), jnp.float32), jnp.cumsum(uf, axis=1)], axis=1)
    t = jnp.arange(n)
    outs = []
    for g, w in enumerate(POOL_WINDOWS):
        lo = jnp.clip(t - w // 2, 0, n)
        hi = jnp.clip(t + w // 2, 0, n)
        seg = csum[:, :, g * POOL_CH:(g + 1) * POOL_CH]
        mean = (seg[:, hi] - seg[:, lo]) / (hi - lo).astype(jnp.float32)[None, :, None]
        outs.append(mean - uf[:, :, g * POOL_CH:(g + 1) * POOL_CH])
    pooled = jnp.stack(outs, axis=2)
    mixed = jnp.einsum('bngc,gcd->bngd', pooled, w_pool.astype(jnp.float32)).reshape(b, n, POOL_WIDTH)
    return (mixed * scale.astype(jnp.float32)).astype(u.dtype)

def split_projection(u):
    b, n, _ = u.shape
    o1 = DA_WIDTH
    o2 = 2 * DA_WIDTH
    o3 = 3 * DA_WIDTH
    o4 = o3 + NA_WIDTH
    o5 = o4 + NA_WIDTH
    o6 = o5 + NA_WIDTH
    qa = u[..., :o1].reshape(b, n, DA_HEADS, 2, DA_QK)
    ka = u[..., o1:o2].reshape(b, n, DA_HEADS, 2, DA_QK)
    va = u[..., o2:o3].reshape(b, n, DA_HEADS, DA_V)
    qb = u[..., o3:o4].reshape(b, n, NA_HEADS, NA_DIM)
    kb = u[..., o4:o5].reshape(b, n, NA_HEADS, NA_DIM)
    vb = u[..., o5:o6].reshape(b, n, NA_HEADS, NA_DIM)
    up = u[..., o6:]
    return qa, ka, va, qb, kb, vb, up

def merge_heads(o_a, o_b, o_c, w_out):
    b, n = o_c.shape[:2]
    cat = jnp.concatenate([o_a.reshape(b, n, DA_WIDTH), o_b.reshape(b, n, NA_WIDTH), o_c], axis=-1)
    return cat @ w_out

def diff_lambda_value(lp, lam_init):
    lp = lp.astype(jnp.float32)
    return jnp.exp(jnp.sum(lp[0] * lp[1])) - jnp.exp(jnp.sum(lp[2] * lp[3])) + lam_init

def moe_ffn(h, w_router, b_router, w_gate, w_up, w_down, ws_gate, ws_up, ws_down):
    shp = h.shape
    t = h.reshape(-1, shp[-1])
    T = t.shape[0]
    s = jax.nn.sigmoid((t @ w_router).astype(jnp.float32))
    sel = s + b_router.astype(jnp.float32)
    per_group = N_EXPERTS // N_GROUPS
    grp_score = lax.top_k(sel.reshape(T, N_GROUPS, per_group), 2)[0].sum(-1)
    _, gidx = lax.top_k(grp_score, TOPK_GROUPS)
    gmask = jnp.any(gidx[:, :, None] == jnp.arange(N_GROUPS)[None, None, :], axis=1)
    emask = jnp.repeat(gmask, per_group, axis=1)
    _, eidx = lax.top_k(jnp.where(emask, sel, -jnp.inf), TOP_K)
    w_sel = jnp.take_along_axis(s, eidx, axis=1)
    w_sel = w_sel / jnp.sum(w_sel, axis=-1, keepdims=True) * ROUTED_SCALE
    gates = jnp.zeros((T, N_EXPERTS), jnp.float32).at[jnp.arange(T)[:, None], eidx].set(w_sel)
    hid = jax.nn.silu(jnp.einsum('td,edf->tef', t, w_gate)) * jnp.einsum('td,edf->tef', t, w_up)
    routed = jnp.einsum('tef,efd->td', hid * gates[:, :, None].astype(hid.dtype), w_down)
    shared = (jax.nn.silu(t @ ws_gate) * (t @ ws_up)) @ ws_down
    return (routed + shared).reshape(shp)

def setup_inputs(seed: int = 0) -> dict:
    key = jax.random.key(seed)
    ks = iter(jax.random.split(key, 40))
    D = D_MODEL

    def nrm(shape, s):
        return jax.random.normal(next(ks), shape, jnp.float32) * s

    return {
        'x_prompt': nrm((BATCH, SEQ, D), 1.0),
        'x_sample': nrm((DEC_BATCH, DEC_SEQ, D), 1.0),
        'cache_diff_k': nrm((DEC_BATCH, DEPTH, PAST_LEN, DA_HEADS, 2 * DA_QK), 1.0),
        'cache_diff_v': nrm((DEC_BATCH, DEPTH, PAST_LEN, DA_HEADS, DA_V), 1.0),
        'cache_na_k': nrm((DEC_BATCH, DEPTH, PAST_LEN, NA_HEADS, NA_DIM), 1.0),
        'cache_na_v': nrm((DEC_BATCH, DEPTH, PAST_LEN, NA_HEADS, NA_DIM), 1.0),
        'c': nrm((DEC_BATCH, D), 1.0),
        'c_ctx': nrm((D,), 1.0),
        'w_ada': nrm((DEPTH, D, 6 * D), 0.5 * D ** -0.5),
        'b_ada': nrm((DEPTH, 6 * D), 0.02),
        'g_pre_mix': 1.0 + nrm((DEPTH, D), 0.02),
        'g_post_mix': 1.0 + nrm((DEPTH, D), 0.02),
        'g_pre_ffn': 1.0 + nrm((DEPTH, D), 0.02),
        'g_post_ffn': 1.0 + nrm((DEPTH, D), 0.02),
        'w_in': nrm((DEPTH, D, IN_COLS), D ** -0.5),
        'w_out': nrm((DEPTH, MIX_WIDTH, D), MIX_WIDTH ** -0.5),
        'diff_lambda': nrm((DEPTH, 4, DA_QK), 0.1),
        'g_diff': 1.0 + nrm((DEPTH, DA_V), 0.02),
        'na_bias': nrm((DEPTH, NA_HEADS, 2 * NA_ROWS - 1, 2 * NA_COLS - 1), 0.1),
        'pool_w': nrm((DEPTH, len(POOL_WINDOWS), POOL_CH, POOL_CH), POOL_CH ** -0.5),
        'pool_scale': 1.0 + nrm((DEPTH, POOL_WIDTH), 0.02),
        'w_router': nrm((DEPTH, D, N_EXPERTS), D ** -0.5),
        'b_router': nrm((DEPTH, N_EXPERTS), 0.01),
        'w_gate': nrm((DEPTH, N_EXPERTS, D, EXPERT_DIM), D ** -0.5),
        'w_up': nrm((DEPTH, N_EXPERTS, D, EXPERT_DIM), D ** -0.5),
        'w_down': nrm((DEPTH, N_EXPERTS, EXPERT_DIM, D), EXPERT_DIM ** -0.5),
        'ws_gate': nrm((DEPTH, D, SHARED_DIM), D ** -0.5),
        'ws_up': nrm((DEPTH, D, SHARED_DIM), D ** -0.5),
        'ws_down': nrm((DEPTH, SHARED_DIM, D), SHARED_DIM ** -0.5),
    }

def reference(x_prompt, x_sample, cache_diff_k, cache_diff_v, cache_na_k, cache_na_v, c, c_ctx,
              w_ada, b_ada, g_pre_mix, g_post_mix, g_pre_ffn, g_post_ffn, w_in, w_out,
              diff_lambda, g_diff, na_bias, pool_w, pool_scale, w_router, b_router,
              w_gate, w_up, w_down, ws_gate, ws_up, ws_down):
    yp = x_prompt
    ys = x_sample
    bp, lp = yp.shape[:2]
    bs, ns = ys.shape[:2]
    new_dk, new_dv, new_nk, new_nv = [], [], [], []
    for li in range(DEPTH):
        lam_init = 0.8 - 0.6 * math.exp(-0.3 * li)
        lam = diff_lambda_value(diff_lambda[li], lam_init)
        m_ctx = modulation(c_ctx[None, :], w_ada[li], b_ada[li])
        m_lat = modulation(c, w_ada[li], b_ada[li])

        h = adaln(rmsnorm(yp, g_pre_mix[li]), m_ctx[0], m_ctx[1])
        qa, ka, va, qb, kb, vb, up = split_projection(h @ w_in[li])
        o_a = rmsnorm(diff_attention(qa, ka, va, lam), g_diff[li]) * (1.0 - lam_init)
        o_b = dense_attention(qb, kb, vb)
        o_c = multiscale_pool(up, pool_w[li], pool_scale[li])
        yp = yp + m_ctx[2] * rmsnorm(merge_heads(o_a, o_b, o_c, w_out[li]), g_post_mix[li])
        h = adaln(rmsnorm(yp, g_pre_ffn[li]), m_ctx[3], m_ctx[4])
        f = moe_ffn(h, w_router[li], b_router[li], w_gate[li], w_up[li], w_down[li],
                    ws_gate[li], ws_up[li], ws_down[li])
        yp = yp + m_ctx[5] * rmsnorm(f, g_post_ffn[li])
        new_dk.append(ka.reshape(bp, lp, DA_HEADS, 2 * DA_QK))
        new_dv.append(va)
        new_nk.append(kb)
        new_nv.append(vb)

        lc = cache_diff_k.shape[2]
        h = adaln(rmsnorm(ys, g_pre_mix[li]), m_lat[0], m_lat[1])
        qa, ka, va, qb, kb, vb, up = split_projection(h @ w_in[li])
        qa = axial_rope(qa.reshape(bs, ns, 2 * DA_HEADS, DA_QK)).reshape(bs, ns, DA_HEADS, 2, DA_QK)
        ka = axial_rope(ka.reshape(bs, ns, 2 * DA_HEADS, DA_QK)).reshape(bs, ns, DA_HEADS, 2, DA_QK)
        ck = cache_diff_k[:, li].reshape(bs, lc, DA_HEADS, 2, DA_QK)
        k_all = jnp.concatenate([ka, ck], axis=1)
        v_all = jnp.concatenate([va, cache_diff_v[:, li]], axis=1)
        o_a = rmsnorm(diff_attention(qa, k_all, v_all, lam), g_diff[li]) * (1.0 - lam_init)
        o_b = neighbourhood_attention(qb, kb, vb, cache_na_k[:, li], cache_na_v[:, li], na_bias[li])
        o_c = multiscale_pool(up, pool_w[li], pool_scale[li])
        ys = ys + m_lat[2] * rmsnorm(merge_heads(o_a, o_b, o_c, w_out[li]), g_post_mix[li])
        h = adaln(rmsnorm(ys, g_pre_ffn[li]), m_lat[3], m_lat[4])
        f = moe_ffn(h, w_router[li], b_router[li], w_gate[li], w_up[li], w_down[li],
                    ws_gate[li], ws_up[li], ws_down[li])
        ys = ys + m_lat[5] * rmsnorm(f, g_post_ffn[li])

    new_diff_k = jnp.stack(new_dk, axis=1)
    new_diff_v = jnp.stack(new_dv, axis=1)
    new_na_k = jnp.stack(new_nk, axis=1)
    new_na_v = jnp.stack(new_nv, axis=1)
    return (yp, ys, new_diff_k, new_diff_v, new_na_k, new_na_v)


_drawn_inputs = setup_inputs


def setup_inputs(seed=0):
    import zlib

    import numpy as np

    out = dict(_drawn_inputs(seed))
    spreads = {}
    factors = {'g_post_ffn': 3.71, 'na_bias': 5.89, 'pool_scale': 3.372}
    for name, (base, spread) in spreads.items():
        noise = np.random.default_rng([zlib.crc32(name.encode()), seed]).standard_normal(out[name].shape)
        drawn = base * np.exp(spread * noise) if base else spread * noise
        out[name] = __import__('jax').numpy.asarray(drawn.astype(out[name].dtype))
    for name, factor in factors.items():
        out[name] = (out[name] * factor).astype(out[name].dtype)
    return out
```

```python
import math
from contextlib import ExitStack

import numpy as np

import concourse.bass as bass
from concourse import mybir

D = 1024
DEPTH = 2
T = 128
NG = 2
PAST = 128
P = 128
KT = D // P
DA_H, DA_QK, DA_V = 4, 64, 128
DA_W = DA_H * DA_V
NA_H, NA_DIM = 4, 64
NA_W = NA_H * NA_DIM
NA_ROWS, NA_COLS, GRID_W = 8, 16, 64
WINDOWS = (2, 4, 8, 16)
POOL_CH = 64
IN_COLS = 3 * DA_W + 3 * NA_W + len(WINDOWS) * POOL_CH
NA_AT = 3 * DA_W
POOL_AT = NA_AT + 3 * NA_W
N_EXP, F = 64, 256
FT = F // P
N_EXP_GROUPS, TOP_GROUPS = 8, 4
ROUTED_SCALE = 2.5
EPS = 1e-6
NEG = -1e30
HALF = 512
SLOTS = 64
PAIRS = N_EXP // 2
ROUNDS = NG * T // SLOTS
VISITS = PAIRS * ROUNDS
NULL = VISITS
BIG = 3e38
ADA = 6
ITEM = 12288
GU, DN = 4096, 8192
BLOCK, RING = 4096, 6
QUARTER = D // 4
BCAST = NG * 4

EARLY = 2
ADA_IN_ATTENTION = (((2, 1), (2, 1)), ((1, 1), (1, 0)))
ADA_AFTER_OUT = (1, 0)



def ada_order(layer):
    out = [("ada", layer, i, a) for i in range(3 if layer else EARLY, ADA) for a in range(2)]
    if layer + 1 < DEPTH:
        out += [("ada", layer + 1, i, a) for i in range(3) for a in range(2)]
    return out


def blocks_before_experts(layer):
    first = [("ada", 0, i, a) for i in range(EARLY) for a in range(2)] if layer == 0 else []
    ada = ada_order(layer)
    n = len(ada) - 2 * ADA_AFTER_OUT[layer]
    assert n == 2 * sum(sum(g) for g in ADA_IN_ATTENTION[layer])
    def split(name, parts):
        return [b for k in range(parts) for b in ((name, k), ("hi", name, k))]
    return first + [("spare", 0), ("spare", 1)] + split("in", 5) + ada[:n] + split("out", 2) + ada[n:] + [("shared_gu",), ("shared_dn",)]


STATIC = [blocks_before_experts(l) for l in range(DEPTH)]
FIRST_BLOCK = [sum(len(b) for b in STATIC[:l]) for l in range(DEPTH)]
SPLIT = [(l, b[1:]) for l, blocks in enumerate(STATIC) for b in blocks if b[0] == "hi"]
VECTORS = [b for blocks in STATIC for b in blocks if b[0] == "ada"]
PAIR_AT = [(FIRST_BLOCK[l] + len(STATIC[l])) % RING for l in range(DEPTH)]
assert all(p % 3 == 0 for p in PAIR_AT)


def const_layout():
    at, where = 0, {}
    for name, n in (("ident", P), ("cos", 64), ("sin", 32), ("band", 4 * P), ("before", 64),
                    ("slot", SLOTS), ("row", 1), ("visit", VISITS), ("earlier", P), ("minus_half", 4)):
        where[name] = (at, n)
        at += n
    return where, at


def program(nc, io):
    f32, f32r, bf16, i32 = mybir.dt.float32, mybir.dt.float32r, mybir.dt.bfloat16, mybir.dt.int32
    ALU, ACT, AX = mybir.AluOpType, mybir.ActivationFunctionType, mybir.AxisListType
    where, n_const = const_layout()

    base = 16512
    cursor = [base]

    def sb(name, shape, dt=f32, at=None):
        size = int(np.prod(shape[1:])) * (2 if dt == bf16 else 4)
        size = (size + 31) // 32 * 32
        start = cursor[0] if at is None else at
        if at is None:
            cursor[0] += size
        assert start + size <= 229344, (name, start + size)
        return nc.alloc_sbuf_tensor_at(name, shape, dt, offset=start)

    W = sb("weights", [P, 2 * ITEM])
    Wr = sb("weights_split", [P, 2 * ITEM], f32r, at=base)
    x = sb("x", [P, NG, D])
    h = sb("h", [P, NG, D])
    hT = sb("hT", [P, KT, NG, T])
    probs = sb("probs", [P, 8, 2 * T], at=cursor[0] - 8192)
    hThi = sb("hT_high", [P, KT, NG, T], f32r, at=cursor[0] - 8192)
    mb = sb("mod_bcast", [P, 3, NG, D])
    modv = sb("mod_rows", [P, ADA, NG, QUARTER])
    raw = sb("mod_raw", [P, QUARTER])
    const = sb("const", [P, n_const])
    nlam = sb("minus_lambda", [P, 4])
    silu_c = sb("silu_c", [P, NG, KT])
    c_in = sb("c_in", [P, NG, KT])
    cb = sb("c_columns", [P, KT, NG, 16])
    ss = sb("sum_squares", [P, 8])
    rstd = sb("rstd", [P, 8])
    mx = sb("row_max", [P, 8])
    nm = sb("minus_max", [P, 8])
    rs = sb("row_sum", [P, 8])
    rr = sb("row_scale", [P, 8])
    vec = sb("bias_and_gain", [P, 2, QUARTER])
    earlier = sb("earlier", [P, P], bf16)
    ones = sb("ones", [P, P], bf16)
    ident16 = sb("ident16", [P, P], bf16)
    shared_region = cursor[0]
    U = sb("U", [P, NG, IN_COLS])
    qkT_at = cursor[0]
    qkT = sb("qkT", [P, 12, T])
    cacheT = sb("cacheT", [P, 6, PAST])
    nab_at = cursor[0]
    nab = sb("na_bias", [P, NA_H, T])
    assert qkT_at + 8192 <= nab_at
    hTlo = sb("hT_low", [P, KT, NG, T], f32r, at=qkT_at)
    cdk = sb("cache_dk", [P, DA_W])
    cdv = sb("cache_dv", [P, DA_W])
    cnk = sb("cache_nk", [P, NA_W])
    cnv = sb("cache_nv", [P, NA_W])
    poolw = sb("pool_w", [P, 2, POOL_CH])
    pscale = sb("pool_scale", [P, 4 * POOL_CH])
    gd = sb("g_diff", [P, DA_V])
    lam4 = sb("lambda_rows", [P, 4, DA_QK])
    sq = cdk[:, :]
    pooledT = cnk[:, :].rearrange("p (w t) -> p w t", w=2)
    wT = probs[:, 4:8, :].rearrange("p h (b q) -> p (h b) q", q=T)
    sall = U[:, 1, 0:4 * 2 * T].rearrange("p (h k) -> p h k", h=NA_H)

    def comb_of(g):
        K = T * (1 + g)
        return U[:, g, 0:DA_H * K].rearrange("p (h k) -> p h k", h=DA_H)

    cursor[0] = shared_region
    x3 = sb("x_parts", [P, NG, 3, KT, P], bf16)
    xgT_at = cursor[0]
    xgT = sb("gathered", [P, 2, KT, P])
    pick = sb("pick", [P, 2, NG, 2 * SLOTS + 8], bf16)
    put = sb("put", [P, 2, NG * T], f32r)
    y_at = cursor[0]
    yhi = sb("y_hi", [P, D], f32r)
    ylo = sb("y_lo", [P, D], f32r)
    silu = sb("silu", [P, F])
    hid = sb("hidden", [P, F])
    hidT = sb("hiddenT", [P, FT, P])
    slot_gate = sb("slot_gate", [P, 2])
    RK = sb("slot_of", [P, NG, 2 * (VISITS + 1)])
    G3 = sb("gate_parts", [P, NG, N_EXP, 3], bf16)
    visits = sb("visits", [1, VISITS + 8], i32)
    n_visits = sb("n_visits", [1, 8], i32)
    shid = sb("shared_hidden", [P, NG, F], at=xgT_at)
    shT = sb("shared_hiddenT", [P, NG, FT, T], at=xgT_at + 2048)
    ssilu = sb("shared_sigmoid", [P, NG, F], at=xgT_at + 4096)
    experts_end = cursor[0]
    cursor[0] = y_at
    wr = sb("w_router", [P, KT, N_EXP])
    s_ = sb("scores", [P, NG, N_EXP])
    sel = sb("sel", [P, NG, N_EXP])
    selm = sb("sel_masked", [P, NG, N_EXP])
    found = sb("found", [P, NG, N_EXP])
    maskf = sb("chosen", [P, NG, N_EXP])
    maskb = sb("chosen16", [P, NG, N_EXP], bf16)
    gates = sb("gates", [P, NG, N_EXP])
    rk = sb("rank", [P, NG, N_EXP])
    t8 = sb("top8_of_group", [P, NG * N_EXP_GROUPS, 8])
    gsc = sb("group_score", [P, NG * N_EXP_GROUPS])
    gm = sb("group_mask", [P, NG * N_EXP_GROUPS])
    top8 = sb("top8", [P, NG, 8])
    cmp1 = sb("cmp1", [P, 8, 8])
    assert cursor[0] <= y_at + 8192
    cursor[0] = xgT_at + 6144
    cmp2 = sb("cmp2", [P, 8, 8])
    nmx = sb("pair_count", [P, PAIRS])
    act_ = sb("active", [P, VISITS])
    assert cursor[0] <= xgT_at + 8192
    cursor[0] = max(experts_end, shared_region)
    incl = sb("active_sum", [P, VISITS])
    pos = sb("position", [P, VISITS])
    brt = sb("b_router", [P, N_EXP])
    item = sb("item", [P, 4])
    wsum = sb("gate_sum", [P, 4])

    C = {k: const[:, a:a + n] for k, (a, n) in where.items()}
    ident = C["ident"]

    ctx = ExitStack()
    with ctx:
        PS = ctx.enter_context(nc.psum_tensor("PS", [P, 8, HALF], f32))

        def sem(name):
            return ctx.enter_context(nc.semaphore(name))

        x_in, const_in, c_loaded = sem("x_in"), sem("const_in"), sem("c_loaded")
        block_in = [sem(f"block_in{k}") for k in range(RING)]
        vec_in, small_in, router_in = sem("vec_in"), sem("small_in"), sem("router_in")
        kv_out, y_out = sem("kv_out"), sem("y_out")
        dve_step, act_step, pool_step = sem("dve_step"), sem("act_step"), sem("pool_step")
        c_silu, c_cols, consts16 = sem("c_silu"), sem("c_cols"), sem("consts16")
        ada_mm, mod_ready, bcast = sem("ada_mm"), sem("mod_ready"), sem("bcast")
        squares, rstd_ready, h_ready = sem("squares"), sem("rstd_ready"), sem("h_ready")
        tr_mm, hT_a, hT_d = sem("tr_mm"), sem("hT_a"), sem("hT_d")
        u_mm, u_a, u_d = sem("u_mm"), sem("u_a"), sem("u_d")
        lam_e_in, lam_e, lam_ready = sem("lam_e_in"), sem("lam_e"), sem("lam_ready")
        rope_done, ct_mm, ct_ready = sem("rope_done"), sem("ct_mm"), sem("ct_ready")
        qk_mm, qk_a, qk_d = sem("qk_mm"), sem("qk_a"), sem("qk_d")
        sd_mm, sd_max, sd_exp, comb_ready = sem("sd_mm"), sem("sd_max"), sem("sd_exp"), sem("comb_ready")
        wt_mm, wt_a, wt_d, pv_mm = sem("wt_mm"), sem("wt_a"), sem("wt_d"), sem("pv_mm")
        oa_sq, oa_ms, oa_rstd = sem("oa_sq"), sem("oa_ms"), sem("oa_rstd")
        pt_mm, pt_ready, pm_mm = sem("pt_mm"), sem("pt_ready"), sem("pm_mm")
        ns_mm, ns_max, ns_exp = sem("ns_mm"), sem("ns_max"), sem("ns_exp")
        nwt_mm, nwt_a, nwt_d, npv_mm, cat_done = sem("nwt_mm"), sem("nwt_a"), sem("nwt_d"), sem("npv_mm"), sem("cat_done")
        wo_mm, resid = sem("wo_mm"), sem("resid")
        w_high, w_low = sem("w_high"), sem("w_low")
        x_hi, x_rest, x_mid, x3_ready = sem("x_hi"), sem("x_rest"), sem("x_mid"), sem("x3_ready")
        rlog_mm, s_ready, mask_ready, rank_mm = sem("rlog_mm"), sem("s_ready"), sem("mask_ready"), sem("rank_mm")
        item_ready, item_mm, table_ready = sem("item_ready"), sem("item_mm"), sem("table_ready")
        sh_mm, sh_silu, sh_hid, sht_mm, shT_ready = sem("sh_mm"), sem("sh_silu"), sem("sh_hid"), sem("sht_mm"), sem("shT_ready")
        sp_passed = sem("sp_passed")
        shd_mm, acc_done = sem("shd_mm"), sem("acc_done")
        LOOP = ("picked", "ga_mm", "xg_a", "xg_d", "gu_mm", "silu_done", "hid_done", "ht_mm", "hidT_done",
                "put_mm", "slots_done", "down_mm", "yhi_done", "ylo_done", "sc_mm",
                "gu_in0", "gu_in1", "dn_in0", "dn_in1")
        L = [{n: sem(f"{n}_{l}") for n in LOOP} for l in range(DEPTH)]

        block = ctx.enter_context(nc.Block())

        def rows(w):
            return w.rearrange("(p j) n -> p (j n)", p=P)

        def pair_at(l, buf):
            return (PAIR_AT[l] + 3 * buf) % RING * BLOCK

        def use_block(engine, layer, what):
            k = next(FIRST_BLOCK[l] + b.index(what) for l, b in enumerate(STATIC) if what in b and layer in (None, l))
            at = ring_of(k)
            engine.wait_ge(block_in[at], 16 * loads_of(k))
            return W[:, at * BLOCK:(at + 1) * BLOCK]

        def ring_of(k):
            return k % RING

        def loads_of(k):
            every = [b for layer in STATIC for b in layer]
            return sum({"shared_gu": 2, "hi": 0, "spare": 0}.get(every[m][0], 1) for m in range(k % RING, k + 1, RING))

        def block_done(engine, k):
            l = max(n for n in range(DEPTH) if FIRST_BLOCK[n] <= k)
            what = STATIC[l][k - FIRST_BLOCK[l]]
            if what[0] == "hi":
                what = what[1:]
            if what[0] == "spare":
                if k - RING >= FIRST_BLOCK[l]:
                    block_done(engine, k - RING)
            elif what[0] == "ada":
                engine.wait_ge(ada_mm, VECTORS.index(what) + 1)
            elif what[0] == "in":
                engine.wait_ge(u_mm, 10 * l + NG * (what[1] + 1))
            elif what[0] == "out":
                engine.wait_ge(wo_mm, NG * (2 * l + what[1] + 1))
            elif what[0] == "shared_gu":
                engine.wait_ge(sh_mm, NG * (l + 1))
            else:
                engine.wait_ge(shd_mm, l + 1)

        def split_block(l, name, part):
            m = SPLIT.index((l, (name, part)))
            k = FIRST_BLOCK[l] + STATIC[l].index((name, part))
            at, hi = ring_of(k) * BLOCK, ring_of(k + 1) * BLOCK
            return m, k, W[:, at:at + BLOCK], Wr[:, at:at + BLOCK], Wr[:, hi:hi + BLOCK]

        def load_pair(sp, l, buf, expert, names=("w_gate", "w_up", "w_down")):
            at = pair_at(l, buf)
            gu = W[:, at:at + 2 * GU].rearrange("p (e g n) -> p e g n", e=2, g=2)
            dn = W[:, at + DN:at + ITEM].rearrange("p (e n) -> p e n", e=2)
            for name in names:
                dst, done = {"w_gate": (gu[:, :, 0, :], "gu_in"), "w_up": (gu[:, :, 1, :], "gu_in"), "w_down": (dn, "dn_in")}[name]
                src = io[name][l, bass.ds(expert, 2), :, :].rearrange("e (p j) n -> p e (j n)", p=P)
                sp.dma_start(dst, src).then_inc(L[l][f"{done}{buf}"], 16)

        @block.sync
        def _(sp):
            sp.dma_start(c_in[:, 0, :], io["c_ctx"].rearrange("(p j) -> p j", p=P)).then_inc(c_loaded, 16)
            sp.dma_start(c_in[:, 1, :], io["c"][0, :].rearrange("(p j) -> p j", p=P)).then_inc(c_loaded, 16)
            for l in range(DEPTH):
                for m, what in enumerate(STATIC[l]):
                    k = FIRST_BLOCK[l] + m
                    at = ring_of(k)
                    if l and m in (0, 5):
                        sp.wait_ge(*((L[l - 1]["gu_mm"], count) if m == 0 else (L[l - 1]["down_mm"], count * 2)))
                        sp.sem_inc(sp_passed, 1)
                    if what[0] in ("hi", "spare"):
                        continue
                    dst = W[:, at * BLOCK:(at + 1) * BLOCK]
                    if m >= RING:
                        block_done(sp, k - RING)

                    def cols(name, layer, a, n):
                        return io[name][layer].rearrange("(p j) n -> p j n", p=P)[:, :, a:a + n]
                    if what[0] == "ada":
                        src = [cols("w_ada", what[1], what[2] * D, D)[:, 4 * what[3]:4 * what[3] + 4, :]]
                    elif what[0] == "in":
                        src = [cols("w_in", l, what[1] * HALF, HALF)]
                    elif what[0] == "out":
                        src = [cols("w_out", l, what[1] * HALF, HALF)]
                    elif what[0] == "shared_gu":
                        src = [cols("ws_gate", l, 0, F), cols("ws_up", l, 0, F)]
                    else:
                        src = [cols("ws_down", l, 0, D)]
                        dst = dst[:, 0:FT * D]
                    each = dst.shape[1] // len(src)
                    for n, from_ in enumerate(src):
                        to = dst[:, n * each:(n + 1) * each].rearrange("p (j n) -> p j n", n=from_.shape[2])
                        sp.dma_start(to, from_).then_inc(block_in[at], 16)
                    if what == VECTORS[2 * EARLY - 1]:
                        sp.dma_start(const[:, :], io["const"]).then_inc(const_in, 16)
                        sp.dma_start(x[:, 0, :], io["x_prompt"][0]).then_inc(x_in, 16)
                        sp.dma_start(x[:, 1, :], io["x_sample"][0]).then_inc(x_in, 16)
                last = FIRST_BLOCK[l] + len(STATIC[l])
                for b in range(2):
                    for names, blocks in ((("w_gate", "w_up"), (0, 1)), (("w_down",), (2,))):
                        for n in blocks:
                            block_done(sp, last - RING + 3 * b + n)
                        load_pair(sp, l, b, 2 * b, names)
                sp.wait_ge(table_ready, l + 1)
                count = sp.value_load(n_visits[0:1, 0:1], min_val=PAIRS, max_val=VISITS)
                with sp.Fori(2, count, 2) as i:
                    for b in range(2):
                        visit = sp.value_load(visits[0:1, bass.ds(i + b, 1)], min_val=0, max_val=NULL)
                        expert = sp.snap((visit & (PAIRS - 1)) * 2)
                        sp.wait_ge(L[l]["gu_mm"], i + (b - 1))
                        sp.sem_inc(sp_passed, 1)
                        load_pair(sp, l, b, expert, ("w_gate", "w_up"))
                        sp.wait_ge(L[l]["down_mm"], i * 2 + 2 * (b - 1))
                        sp.sem_inc(sp_passed, 1)
                        load_pair(sp, l, b, expert, ("w_down",))
            for g, name in enumerate(("y_prompt", "y_sample")):
                sp.wait_ge(resid, 2 * NG * DEPTH)
                sp.dma_start(io[name][0], x[:, g, :]).then_inc(y_out, 16)
            sp.wait_ge(y_out, 32)
            sp.wait_ge(kv_out, 64 * DEPTH)

        @block.gpsimd
        def _(pool):
            broadcasts, steps = [0], [0]

            def idle():
                if broadcasts[0]:
                    pool.wait_ge(bcast, broadcasts[0])
                if steps[0]:
                    pool.wait_ge(pool_step, steps[0])

            def step(ins):
                ins.then_inc(pool_step, 1)
                steps[0] += 1

            def broadcast(part, k):
                idle()
                for g in range(NG):
                    for q in range(4):
                        nc.gpsimd.partition_broadcast(mb[:, k, g, q * QUARTER:(q + 1) * QUARTER],
                                                      modv[32 * q:32 * q + 1, 3 * part + k, g, :]).then_inc(bcast, 1)
                        broadcasts[0] += 1

            def root(q):
                idle()
                for g in range(NG):
                    pool.wait_ge(squares, NG * q + g + 1)
                    step(nc.gpsimd.tensor_scalar(rstd[:, g:g + 1], ss[:, g:g + 1], EPS, None, ALU.add))
                    pool.wait_ge(pool_step, steps[0])
                    nc.gpsimd.tensor_tensor(rstd[:, g:g + 1], rstd[:, g:g + 1], C["minus_half"][:, 0:1], ALU.pow).then_inc(rstd_ready, 1)
                pool.wait_ge(rstd_ready, NG * (q + 1))

            def root_of_heads(n):
                idle()
                pool.wait_ge(oa_ms, n)
                nc.gpsimd.tensor_tensor(rstd[:, 4:8], rstd[:, 4:8], C["minus_half"], ALU.pow).then_inc(oa_rstd, 1)
                pool.wait_ge(oa_rstd, n)

            pool.dma_start(vec[:, :, :], io["vec_rows"]).then_inc(vec_in, 16)
            pool.wait_ge(mod_ready, 1)
            broadcast(0, 0)
            pool.wait_ge(const_in, 16)
            root(0)
            pool.wait_ge(mod_ready, 2)
            broadcast(0, 1)
            for l in range(DEPTH):
                def small(dst, src):
                    pool.dma_start(dst, src).then_inc(small_in, 16)
                small(cdk[:, :], io["cache_diff_k"][0, l].rearrange("t h d -> t (h d)"))
                small(cdv[:, :], io["cache_diff_v"][0, l].rearrange("t h d -> t (h d)"))
                small(cnk[:, :], io["cache_na_k"][0, l].rearrange("t h d -> t (h d)"))
                small(cnv[:, :], io["cache_na_v"][0, l].rearrange("t h d -> t (h d)"))
                small(nab[:, :, :], io["na_bias_grid"][l])
                for par in range(2):
                    small(poolw[64 * par:64 * par + 64, :, :],
                          io["pool_w"][l].rearrange("(a b) c d -> b c a d", b=2)[par])
                small(pscale[:, :], io["pool_scale"][l].partition_broadcast(P))
                small(gd[:, :], io["g_diff"][l].partition_broadcast(P))
                small(lam4[:, :, :], io["diff_lambda"][l].partition_broadcast(P))
                pool.wait_ge(u_d, 5 * l + 2)
                qk = U[:, 1, 0:2 * DA_W]
                heads = 2 * DA_W // 64
                by_head = "p (h d) -> p h d"
                cos = C["cos"].unsqueeze(1).to_broadcast([P, heads, 64])
                sin = C["sin"].rearrange("p (a f) -> p a f", a=2).unsqueeze(1).to_broadcast([P, heads, 2, 16])
                parts = "p (h a b f) -> p h a b f"
                qk5 = qk.rearrange(parts, h=heads, a=2, b=2)
                tmp5 = probs[:, 0:4, :].rearrange("p k c -> p (k c)").rearrange(parts, h=heads, a=2, b=2)
                pool.wait_ge(u_mm, 10 * (l + 1))
                idle()
                for b in range(2):
                    step(nc.gpsimd.tensor_tensor(tmp5[:, :, :, b, :], qk5[:, :, :, 1 - b, :], sin, ALU.mult))
                idle()
                step(nc.gpsimd.tensor_tensor(qk.rearrange(by_head, h=heads), qk.rearrange(by_head, h=heads), cos, ALU.mult))
                idle()
                step(nc.gpsimd.tensor_tensor(qk5[:, :, :, 0, :], qk5[:, :, :, 0, :], tmp5[:, :, :, 0, :], ALU.subtract))
                step(nc.gpsimd.tensor_tensor(qk5[:, :, :, 1, :], qk5[:, :, :, 1, :], tmp5[:, :, :, 1, :], ALU.add))
                idle()
                pool.sem_inc(rope_done, 1)
                pool.wait_ge(u_a, 5 * (l + 1))
                for name, at, n in (("new_diff_k", DA_W, DA_W), ("new_diff_v", 2 * DA_W, DA_W),
                                    ("new_na_k", NA_AT + NA_W, NA_W), ("new_na_v", NA_AT + 2 * NA_W, NA_W)):
                    pool.dma_start(io[name][0, l].rearrange("t h d -> t (h d)"), U[:, 0, at:at + n]).then_inc(kv_out, 16)
                if l == 0:
                    pool.wait_ge(mod_ready, 3)
                    broadcast(0, 2)
                root_of_heads(NG * l + 1)
                for k in range(2):
                    pool.wait_ge(mod_ready, ADA * l + 4 + k)
                    broadcast(1, k)
                root_of_heads(NG * l + 2)
                root(4 * l + 1)
                pool.wait_ge(kv_out, 64 * (l + 1))
                pool.dma_start(wr[:, :, :], rows(io["w_router"][l]).rearrange("p (j e) -> p j e", j=KT)).then_inc(router_in, 16)
                pool.dma_start(brt[:, :], io["b_router"][l].partition_broadcast(P)).then_inc(router_in, 16)
                root(4 * l + 2)
                pool.wait_ge(mod_ready, ADA * (l + 1))
                pool.wait_ge(resid, NG * (2 * l + 1))
                broadcast(1, 2)
                if l + 1 < DEPTH:
                    for k in range(2):
                        pool.wait_ge(mod_ready, ADA * (l + 1) + k + 1)
                        pool.wait_ge(h_ready, NG * 2 * (l + 1))
                        broadcast(0, k)
                root(4 * l + 3)
                if l + 1 < DEPTH:
                    root(4 * l + 4)
                    pool.wait_ge(mod_ready, ADA * (l + 1) + 3)
                    pool.wait_ge(resid, NG * 2 * (l + 1))
                    broadcast(0, 2)

        @block.tensor
        def _(pe):
            mm = nc.tensor.matmul

            def transpose_rows(g, banks):
                for j in range(KT):
                    src = h[:, g, :].rearrange("t (p j) -> t j p", j=KT)[:, j, :]
                    last = nc.tensor.transpose(PS[:, banks + j // 4, (j % 4) * P:(j % 4 + 1) * P], src, ident)
                last.then_inc(tr_mm, 1)

            def hT_wait(r, g):
                pe.wait_ge(hT_a, NG * r + g + 1)
                pe.wait_ge(hT_d, NG * r + g + 1)

            def attention(l, g):
                n = NG * l + g + 1
                K = T * (1 + g)
                nb = 1 + g
                if g:
                    pe.wait_ge(cat_done, NG * l + 1)
                    pe.wait_ge(rope_done, l + 1)
                for k in range(12):
                    if k < 8:
                        src = U[:, g, k * P:(k + 1) * P]
                    else:
                        src = U[:, g, NA_AT + (k - 8) * P:NA_AT + (k - 7) * P]
                    last = nc.tensor.transpose(PS[:, k // 4, (k % 4) * P:(k % 4 + 1) * P], src, ident)
                last.then_inc(qk_mm, 1)
                pe.wait_ge(qk_a, n)
                pe.wait_ge(qk_d, n)
                if g:
                    pe.wait_ge(ct_ready, l + 1)
                for hh in range(DA_H):
                    for m in range(2):
                        r0 = 64 * m
                        if g == 0:
                            last = mm(PS[:, 3 + m, hh * T:(hh + 1) * T], qkT[r0:r0 + 64, hh, :], qkT[r0:r0 + 64, 4 + hh, :], start=True, stop=True)
                        else:
                            bank, col = 3 + 2 * m + hh // 2, (hh % 2) * K
                            mm(PS[:, bank, col:col + T], qkT[r0:r0 + 64, hh, :], qkT[r0:r0 + 64, 4 + hh, :], start=True, stop=True)
                            last = mm(PS[:, bank, col + T:col + K], qkT[r0:r0 + 64, hh, :], cacheT[r0:r0 + 64, hh, :], start=True, stop=True)
                last.then_inc(sd_mm, 1)
                for w in range(4):
                    last = mm(PS[64 * (w % 2):64 * (w % 2) + 64, 2, (w // 2) * T:(w // 2 + 1) * T],
                              U[:, g, POOL_AT + w * POOL_CH:POOL_AT + (w + 1) * POOL_CH],
                              C["band"][:, w * P:(w + 1) * P], start=True, stop=True)
                last.then_inc(pt_mm, 1)
                modulation(l, ADA_IN_ATTENTION[l][g][0], (0, 7))
                pe.wait_ge(comb_ready, n)
                for k in range(DA_H * nb):
                    last = nc.tensor.transpose(PS[:, k // 4, (k % 4) * P:(k % 4 + 1) * P],
                                               comb_of(g)[:, k // nb, (k % nb) * P:(k % nb + 1) * P], ident)
                last.then_inc(wt_mm, 1)
                pe.wait_ge(wt_a, n)
                if g:
                    pe.wait_ge(wt_d, l + 1)
                pe.wait_ge(pt_ready, n)
                for hh in range(DA_H):
                    for b in range(nb):
                        v = cdv[:, hh * DA_V:(hh + 1) * DA_V] if b else U[:, g, 2 * DA_W + hh * DA_V:2 * DA_W + (hh + 1) * DA_V]
                        last = mm(PS[:, 2, hh * DA_V:(hh + 1) * DA_V], wT[:, hh * nb + b, :], v, start=b == 0, stop=b == nb - 1)
                last.then_inc(pv_mm, 1)
                pe.wait_ge(sd_exp, n)
                for hh in range(NA_H // 2):
                    for par in range(2):
                        r0 = 64 * par
                        col = hh * K
                        last = mm(PS[:, 5 + par, col:col + T], qkT[r0:r0 + 64, 8 + hh, :], qkT[r0:r0 + 64, 10 + hh, :], start=True, stop=True)
                        if g:
                            last = mm(PS[:, 5 + par, col + T:col + K], qkT[r0:r0 + 64, 8 + hh, :], cacheT[r0:r0 + 64, 4 + hh, :], start=True, stop=True)
                last.then_inc(ns_mm, 1)
                for w in range(4):
                    r0 = 64 * (w % 2)
                    last = mm(PS[:, w % 2, (w // 2) * POOL_CH:(w // 2 + 1) * POOL_CH], pooledT[r0:r0 + 64, w // 2, :],
                              poolw[r0:r0 + 64, w // 2, :], start=True, stop=True)
                last.then_inc(pm_mm, 1)
                modulation(l, ADA_IN_ATTENTION[l][g][1], (7,))
                pe.wait_ge(ns_exp, n)
                for k in range(NA_H * nb):
                    last = nc.tensor.transpose(PS[:, 3 + k // 4, (k % 4) * P:(k % 4 + 1) * P],
                                               probs[:, k // nb, (k % nb) * P:(k % nb + 1) * P], ident)
                last.then_inc(nwt_mm, 1)
                pe.wait_ge(nwt_a, n)
                if g:
                    pe.wait_ge(nwt_d, l + 1)
                for k in range(NA_H):
                    head = 2 * (k % 2) + k // 2
                    for b in range(nb):
                        v = cnv[:, head * NA_DIM:(head + 1) * NA_DIM] if b else \
                            U[:, g, NA_AT + 2 * NA_W + head * NA_DIM:NA_AT + 2 * NA_W + (head + 1) * NA_DIM]
                        last = mm(PS[:, 5, k * NA_DIM:(k + 1) * NA_DIM], wT[:, k * nb + b, :], v,
                                  start=b == 0, stop=b == nb - 1)
                last.then_inc(npv_mm, 1)

            def split_product(l, name, part, r, banks, done):
                m, k, _, lo, hi = split_block(l, name, part)
                pe.wait_ge(w_high, m + 1)
                for rows_, w, start in ((hThi, hi, True), (hTlo, hi, False), (hThi, lo, False)):
                    if w is lo:
                        pe.wait_ge(w_low, m + 1)
                    for g in range(NG):
                        if start:
                            pe.wait_ge(hT_a, NG * r + g + 1)
                            if banks[g] == 3:
                                pe.wait_ge(hT_d, NG * (r + 1))
                        elif rows_ is hTlo:
                            pe.wait_ge(hT_d, NG * r + g + 1)
                        for j in range(KT):
                            last = mm(PS[:, banks[g], :], rows_[:, j, g, :], w[:, j * HALF:(j + 1) * HALF],
                                      start=start and j == 0, stop=w is lo and j == KT - 1, skip_group_check=True)
                        if w is lo:
                            last.then_inc(done, 1)

            pending = [ada_order(l) for l in range(DEPTH)]
            started = [0]
            last_in = {}

            def modulate(halves, bank):
                if bank in last_in:
                    pe.wait_ge(mod_ready, last_in[bank])
                started[0] += 1
                last_in[bank] = started[0]
                for what in halves:
                    w = use_block(pe, None, what).rearrange("p (j n) -> p j n", n=D)
                    for j in range(4):
                        for q in range(4):
                            jj = 4 * what[3] + j
                            last = mm(PS[32 * q:32 * q + 32, bank, 0:QUARTER], cb[:, jj, :, :].rearrange("p g c -> p (g c)"),
                                      w[:, j, q * QUARTER:(q + 1) * QUARTER], start=jj == 0, stop=jj == KT - 1,
                                      tile_position=(0, 32 * q))
                    last.then_inc(ada_mm, 1)

            def modulation(l, n, banks):
                for k in range(n):
                    modulate([pending[l].pop(0) for _ in range(2)], banks[k])

            pe.wait_ge(c_cols, 1)
            for k in range(EARLY):
                modulate(STATIC[0][2 * k:2 * k + 2], k)
            for l in range(DEPTH):
                S = L[l]
                if l:
                    pe.wait_ge(resid, 2 * NG * l)
                pe.wait_ge(const_in, 16)
                pe.wait_ge(mod_ready, started[0])
                for g in range(NG):
                    pe.wait_ge(h_ready, NG * 2 * l + g + 1)
                    transpose_rows(g, 2 * g)
                for n in range(5):
                    for g in range(NG):
                        if n == 4:
                            pe.wait_ge((u_a, u_d)[g], 5 * l + 1)
                    split_product(l, "in", n, 3 * l, [(4 + 2 * n + g) % 8 for g in range(NG)], u_mm)
                pe.wait_ge(u_a, 5 * (l + 1))
                pe.wait_ge(u_d, 5 * (l + 1))
                pe.wait_ge(small_in, 160 * (l + 1))
                for k in range(6):
                    src = cdk[:, k * P:(k + 1) * P] if k < 4 else cnk[:, (k - 4) * P:(k - 3) * P]
                    last = nc.tensor.transpose(PS[:, 6 + k // 4, (k % 4) * P:(k % 4 + 1) * P], src, ident)
                last.then_inc(ct_mm, 1)
                pe.wait_ge(ct_ready, l + 1)
                attention(l, 0)
                attention(l, 1)
                for g in range(NG):
                    pe.wait_ge(cat_done, NG * l + g + 1)
                    transpose_rows(g, 2 * g)
                for n in range(2):
                    split_product(l, "out", n, 3 * l + 1, [5 + n, 3 + n], wo_mm)
                modulation(l, ADA_AFTER_OUT[l], (7,))
                assert not pending[l]
                for g in range(NG):
                    pe.wait_ge(h_ready, NG * (2 * l + 1) + g + 1)
                    transpose_rows(g, 2 * g)
                hT_wait(3 * l + 2, 1)
                wsg = use_block(pe, l, ("shared_gu",)).rearrange("p (g j n) -> p g j n", g=2, j=KT)
                for g in range(NG):
                    for j in range(KT):
                        last = mm(PS[:, 4 + g, :].rearrange("p (a n) -> p a n", a=2), hT[:, j, g, :], wsg[:, :, j, :],
                                  start=j == 0, stop=j == KT - 1)
                    last.then_inc(sh_mm, 1)
                pe.wait_ge(router_in, 32 * (l + 1))
                pe.wait_ge(mod_ready, started[0])
                for g in range(NG):
                    for j in range(KT):
                        last = mm(PS[:, 7, g * N_EXP:(g + 1) * N_EXP], hT[:, j, g, :], wr[:, j, :], start=j == 0, stop=j == KT - 1)
                last.then_inc(rlog_mm, 1)
                pe.wait_ge(sh_hid, NG * (l + 1))
                for g in range(NG):
                    for j in range(FT):
                        src = shid[:, g, :].rearrange("t (p j) -> t j p", j=FT)[:, j, :]
                        last = nc.tensor.transpose(PS[:, 6, (2 * g + j) * P:(2 * g + j + 1) * P], src, ident)
                last.then_inc(sht_mm, 1)
                pe.wait_ge(shT_ready, l + 1)
                wsd = use_block(pe, l, ("shared_dn",))
                for g in range(NG):
                    for n in range(2):
                        for j in range(FT):
                            last = mm(PS[:, 2 * g + n, :], shT[:, g, j, :],
                                      wsd[:, j * D + n * HALF:j * D + (n + 1) * HALF],
                                      start=j == 0, stop=j == FT - 1, skip_group_check=True)
                last.then_inc(shd_mm, 1)
                pe.wait_ge(mask_ready, l + 1)
                mm(PS[:, 7, 128:192], earlier[:, :], maskb[:, 0, :], start=True, stop=True)
                mm(PS[:, 7, 192:256], earlier[:, :], maskb[:, 1, :], start=True, stop=False)
                mm(PS[:, 7, 192:256], ones[:, :], maskb[:, 0, :], start=False, stop=True)
                mm(PS[:, 7, 256:320], ones[:, :], maskb[:, 0, :], start=True, stop=False)
                mm(PS[:, 7, 256:320], ones[:, :], maskb[:, 1, :], start=False, stop=True).then_inc(rank_mm, 1)
                pe.wait_ge(item_ready, l + 1)
                mm(PS[0:1, 7, 320:448], item[:, 0:1], ident, start=True, stop=True).then_inc(item_mm, 1)

                def gather(u, half):
                    for j in range(4):
                        jj = 4 * half + j
                        for g in range(NG):
                            for part in range(3):
                                last = mm(PS[:, 5, j * P:(j + 1) * P], x3[:, g, part, jj, :], pick[:, u % 2, g, 0:P],
                                          start=(g, part) == (0, 0), stop=(g, part) == (1, 2), skip_group_check=True)
                    last.then_inc(S["ga_mm"], 1)

                def scatter_prep(u):
                    for g in range(NG):
                        nc.tensor.transpose(PS[:, 6, 64 * g:64 * (g + 1)].bitcast(bf16), pick[:, u % 2, g, 0:P], ident16[:, :])
                    for g in range(NG):
                        last = mm(PS[:, 6, 128:134], pick[:, u % 2, g, 0:P], pick[:, u % 2, g, P:P + 6],
                                  start=g == 0, stop=g == NG - 1, skip_group_check=True)
                    last.then_inc(S["put_mm"], 1)

                def scatter(u):
                    for g in range(NG):
                        for part, y in enumerate((yhi, ylo)):
                            for n in range(2):
                                last = mm(PS[:, 2 * g + n, :], put[:, u % 2, g * T:(g + 1) * T], y[:, n * HALF:(n + 1) * HALF],
                                          start=False, stop=False, skip_group_check=True)
                    last.then_inc(S["sc_mm"], 1)

                def gate_up(b, js):
                    w = W[:, pair_at(l, b):pair_at(l, b) + 2 * GU].rearrange("p (e g j n) -> p e g j n", e=2, g=2, j=KT)
                    for j in js:
                        for e in range(2):
                            last = mm(PS[64 * e:64 * e + 64, 4, :].rearrange("p (a n) -> p a n", a=2),
                                      xgT[:, b, j, 64 * e:64 * e + 64], w[:, e, :, j, :],
                                      start=j == 0, stop=j == KT - 1, skip_group_check=True)
                    return last

                pe.wait_ge(x3_ready, NG * (l + 1))
                pe.wait_ge(table_ready, l + 1)
                count = pe.value_load(n_visits[0:1, 0:1], min_val=PAIRS, max_val=VISITS)
                pe.wait_ge(S["picked"], 1)
                gather(0, 0)
                scatter_prep(0)
                pe.wait_ge(S["xg_a"], 1)
                gather(0, 1)
                pe.wait_ge(S["picked"], 2)
                pe.wait_ge(S["xg_d"], 1)
                gather(1, 0)
                with pe.Fori(0, count, 2) as i:
                    for b in range(2):
                        pe.wait_ge(S[f"gu_in{b}"], i * 16 + 32)
                        pe.wait_ge(S["xg_a"], i + (b + 1))
                        pe.wait_ge(S["xg_d"], i + (b + 1))
                        pe.wait_ge(S["ylo_done"], i * 2 + (2 * b + 2))
                        gate_up(b, range(4))
                        pe.wait_ge(S["xg_a"], i + (b + 2))
                        gather(b + 1, 1)
                        gate_up(b, range(4, KT)).then_inc(S["gu_mm"], 1)
                        pe.wait_ge(S["slots_done"], i + (b + 1))
                        scatter(b + 1)
                        scatter_prep(b + 1)
                        pe.wait_ge(S["hid_done"], i + (b + 1))
                        for j in range(FT):
                            src = hid[:, :].rearrange("t (p j) -> t j p", j=FT)[:, j, :]
                            last = nc.tensor.transpose(PS[:, 7, j * P:(j + 1) * P], src, ident)
                        last.then_inc(S["ht_mm"], 1)
                        pe.wait_ge(S["hidT_done"], i + (b + 1))
                        pe.wait_ge(S["slots_done"], i + (b + 2))
                        pe.wait_ge(S[f"dn_in{b}"], i * 8 + 16)
                        w = W[:, pair_at(l, b) + DN:pair_at(l, b) + ITEM].rearrange("p (e j n) -> p e j n", e=2, j=FT)
                        for n, bank in enumerate((6, 4)):
                            for j in range(FT):
                                for e in range(2):
                                    last = mm(PS[64 * e:64 * e + 64, bank, :], hidT[:, j, 64 * e:64 * e + 64],
                                              w[:, e, j, n * HALF:(n + 1) * HALF], start=j == 0, stop=j == FT - 1,
                                              skip_group_check=True)
                            last.then_inc(S["down_mm"], 1)
                        pe.wait_ge(S["picked"], i + (b + 3))
                        pe.wait_ge(S["xg_d"], i + (b + 2))
                        gather(b, 0)
                pe.wait_ge(S["ylo_done"], count * 2 + 2)
                scatter(1)
                pe.wait_ge(S["sc_mm"], count + 1)
                mm(PS[0:1, 7, 0:1], ident[:, 0:1], ident[:, 0:1], start=True, stop=True).then_inc(acc_done, 1)

        @block.scalar
        def _(act):
            run = nc.scalar.activation

            def rows_out(r):
                for g in range(NG):
                    act.wait_ge(tr_mm, NG * r + g + 1)
                    run(hT[:, 0:4, g, :], PS[:, 2 * g, :].rearrange("p (j t) -> p j t", j=4), ACT.Copy).then_inc(hT_a, 1)

            def high_rows(r):
                for g in range(NG):
                    act.wait_ge(tr_mm, NG * r + g + 1)
                    for b in range(2):
                        last = run(hThi[:, 4 * b:4 * b + 4, g, :], PS[:, 2 * g + b, :].rearrange("p (j t) -> p j t", j=4), ACT.Copy)
                    last.then_inc(hT_a, 1)

            def high_weights(l, name, part):
                m, k, w, _, hi = split_block(l, name, part)
                if k + 1 - RING >= FIRST_BLOCK[l]:
                    block_done(act, k + 1 - RING)
                act.wait_ge(block_in[ring_of(k)], 16 * loads_of(k))
                run(hi, w, ACT.Copy).then_inc(w_high, 1)

            def norm_squares(src, ready=None, count=0):
                for g in range(NG):
                    if ready is not None:
                        act.wait_ge(ready, count + g + 1)
                    run(h[:, g, :], src(g), ACT.Square, scale=D ** -0.5, accum_out=ss[:, g:g + 1]).then_inc(squares, 1)

            def attention(l, g):
                n = NG * l + g + 1
                K, nb = T * (1 + g), 1 + g
                act.wait_ge(qk_mm, n)
                run(qkT[:, 0:4, :], PS[:, 0, :].rearrange("p (k t) -> p k t", k=4), ACT.Copy)
                run(qkT[:, 8:12, :], PS[:, 2, :].rearrange("p (k t) -> p k t", k=4), ACT.Copy).then_inc(qk_a, 1)
                act.wait_ge(pt_mm, n)
                run(pooledT, PS[:, 2, 0:256].rearrange("p (w t) -> p w t", w=2), ACT.Copy).then_inc(pt_ready, 1)
                act.wait_ge(sd_max, n)
                if g == 0:
                    act.wait_ge(rope_done, l + 1)
                for k in range(8):
                    src = PS[:, 3 + k // 4, (k % 4) * K:(k % 4 + 1) * K] if g == 0 else PS[:, 3 + k // 2, (k % 2) * K:(k % 2 + 1) * K]
                    last = run(probs[:, k, 0:K], src, ACT.Exp, bias=nm[:, k:k + 1], scale=DA_QK ** -0.5, accum_out=rs[:, k:k + 1])
                last.then_inc(sd_exp, 1)
                act.wait_ge(wt_mm, n)
                run(wT[:, 0:4, :], PS[:, 0, :].rearrange("p (k t) -> p k t", k=4), ACT.Copy).then_inc(wt_a, 1)
                act.wait_ge(pv_mm, n)
                run(sq, PS[:, 2, :], ACT.Square).then_inc(oa_sq, 1)
                act.wait_ge(ns_max, n)
                for k in range(NA_H):
                    src = PS[:, 5 + k // 2, (k % 2) * K:(k % 2 + 1) * K] if g == 0 else sall[:, k, :]
                    last = run(probs[:, k, 0:K], src, ACT.Exp, bias=nm[:, k:k + 1],
                               scale=NA_DIM ** -0.5 if g == 0 else 1.0, accum_out=rs[:, k:k + 1])
                last.then_inc(ns_exp, 1)
                act.wait_ge(nwt_mm, n)
                run(wT[:, 0:4, :], PS[:, 3, :].rearrange("p (k t) -> p k t", k=4), ACT.Copy).then_inc(nwt_a, 1)

            act.wait_ge(c_loaded, 32)
            run(silu_c[:, :, :], c_in[:, :, :], ACT.Silu).then_inc(c_silu, 1)
            for l in range(DEPTH):
                S = L[l]
                if l == 0:
                    act.wait_ge(x_in, 32)
                    norm_squares(lambda g: x[:, g, :])
                else:
                    norm_squares(lambda g: x[:, g, :], resid, NG * (2 * l - 1))
                high_weights(l, "in", 0)
                high_rows(3 * l)
                high_weights(l, "in", 1)
                act.wait_ge(lam_e_in, l + 1)
                run(nlam[:, 2:4], nlam[:, 2:4], ACT.Exp).then_inc(lam_e, 1)
                for n in range(5):
                    act.wait_ge(u_mm, 10 * l + 2 * n + 1)
                    run(U[:, 0, n * HALF:(n + 1) * HALF], PS[:, (4 + 2 * n) % 8, :], ACT.Copy).then_inc(u_a, 1)
                    if n < 3:
                        high_weights(l, "in", n + 2)
                act.wait_ge(ct_mm, l + 1)
                run(cacheT[:, 0:4, :], PS[:, 6, :].rearrange("p (k t) -> p k t", k=4), ACT.Copy)
                run(cacheT[:, 4:6, :], PS[:, 7, 0:256].rearrange("p (k t) -> p k t", k=2), ACT.Copy).then_inc(ct_ready, 1)
                attention(l, 0)
                attention(l, 1)
                high_weights(l, "out", 0)
                high_rows(3 * l + 1)
                high_weights(l, "out", 1)
                act.wait_ge(wo_mm, 2 * NG * (l + 1))
                norm_squares(lambda g: PS[:, 5 - 2 * g:7 - 2 * g, :].rearrange("p a n -> p (a n)"))
                norm_squares(lambda g: x[:, g, :], resid, 2 * NG * l)
                rows_out(3 * l + 2)
                act.wait_ge(kv_out, 64 * (l + 1))
                for g in range(NG):
                    run(x3[:, g, 0, :, :], h[:, g, :].rearrange("t (p j) -> t j p", j=KT), ACT.Copy).then_inc(x_hi, 1)
                for g in range(NG):
                    act.wait_ge(x_rest, NG * l + g + 1)
                    run(x3[:, g, 1, :, :], h[:, g, :].rearrange("t (p j) -> t j p", j=KT), ACT.Copy).then_inc(x_mid, 1)
                for g in range(NG):
                    act.wait_ge(sh_mm, NG * l + g + 1)
                    run(ssilu[:, g, :], PS[:, 4 + g, 0:F], ACT.Sigmoid).then_inc(sh_silu, 1)
                act.wait_ge(rlog_mm, l + 1)
                run(s_[:, :, :], PS[:, 7, 0:NG * N_EXP].rearrange("p (g e) -> p g e", g=NG), ACT.Sigmoid).then_inc(s_ready, 1)
                act.wait_ge(sht_mm, l + 1)
                run(shT[:, :, :, :], PS[:, 6, :].rearrange("p (g j t) -> p g j t", g=NG, j=FT), ACT.Copy).then_inc(shT_ready, 1)

                def gathered(b, half):
                    return xgT[:, b, 4 * half:4 * half + 4, :], PS[:, 5, :].rearrange("p (j s) -> p j s", j=4)

                act.wait_ge(table_ready, l + 1)
                run(silu[:, 0:P], ident, ACT.Silu).then_inc(act_step, 1)
                act.wait_ge(act_step, l + 1)
                count = act.value_load(n_visits[0:1, 0:1], min_val=PAIRS, max_val=VISITS)
                act.wait_ge(S["ga_mm"], 1)
                run(*gathered(0, 0), ACT.Copy).then_inc(S["xg_a"], 1)
                act.wait_ge(S["ga_mm"], 3)
                run(*gathered(1, 0), ACT.Copy).then_inc(S["xg_a"], 1)
                with act.Fori(0, count, 2) as i:
                    for b in range(2):
                        act.wait_ge(S["gu_mm"], i + (b + 1))
                        run(silu[:, :], PS[:, 4, 0:F], ACT.Silu).then_inc(S["silu_done"], 1)
                        act.wait_ge(S["ht_mm"], i + (b + 1))
                        run(hidT[:, :, :], PS[:, 7, 0:F].rearrange("p (j s) -> p j s", j=FT), ACT.Copy).then_inc(S["hidT_done"], 1)
                        for n, bank in enumerate((6, 4)):
                            act.wait_ge(S["down_mm"], i * 2 + (2 * b + n + 1))
                            run(yhi[:, n * HALF:(n + 1) * HALF], PS[:, bank, :], ACT.Copy).then_inc(S["yhi_done"], 1)
                        act.wait_ge(S["ga_mm"], i * 2 + (2 * b + 5))
                        run(*gathered(b, 0), ACT.Copy).then_inc(S["xg_a"], 1)
                act.wait_ge(acc_done, l + 1)
                norm_squares(lambda g: PS[:, 2 * g:2 * g + 2, :].rearrange("p a n -> p (a n)"))

        @block.vector
        def _(dve):
            v = nc.vector
            steps = [0]

            def step(ins):
                ins.then_inc(dve_step, 1)
                steps[0] += 1

            def settled():
                dve.wait_ge(dve_step, steps[0])

            def rows_out(r):
                for g in range(NG):
                    dve.wait_ge(tr_mm, NG * r + g + 1)
                    v.tensor_copy(hT[:, 4:8, g, :], PS[:, 2 * g + 1, :].rearrange("p (j t) -> p j t", j=4)).then_inc(hT_d, 1)

            def low_rows(r):
                for g in range(NG):
                    dve.wait_ge(hT_a, NG * r + g + 1)
                    for b in range(2):
                        js = slice(4 * b, 4 * b + 4)
                        last = v.tensor_tensor(hTlo[:, js, g, :], PS[:, 2 * g + b, :].rearrange("p (j t) -> p j t", j=4),
                                               hThi[:, js, g, :].bitcast(f32), ALU.subtract)
                    last.then_inc(hT_d, 1)

            def low_weights(l, name, part):
                m, _, w, lo, hi = split_block(l, name, part)
                dve.wait_ge(w_high, m + 1)
                v.tensor_tensor(lo, w, hi.bitcast(f32), ALU.subtract).then_inc(w_low, 1)

            vectors = [0]

            def finish_vector(bank):
                m = vectors[0]
                vectors[0] += 1
                _, layer, i, _ = VECTORS[2 * m]
                if layer:
                    dve.wait_ge(bcast, BCAST * (ADA * layer if i >= 3 else ADA * layer - 3))
                dve.wait_ge(vec_in, 16)
                if m:
                    dve.wait_ge(mod_ready, m)
                dve.wait_ge(ada_mm, 2 * m + 2)
                step(v.tensor_tensor(raw[:, :], PS[:, bank, 0:QUARTER], vec[:, 0, :], ALU.add))
                settled()
                if i % 3:
                    step(v.scalar_tensor_tensor(raw[:, :], raw[:, :], float(i % 3 == 1), vec[:, 1, :], ALU.add, ALU.mult))
                    settled()
                for g in range(NG):
                    last = v.stream_shuffle(modv[:, i, g, :], raw[:, :], [16 * g + ADA * layer + i] * 32)
                last.then_inc(mod_ready, 1)

            def pre_norm(q, bcasts):
                for g in range(NG):
                    dve.wait_ge(rstd_ready, NG * q + g + 1)
                    dve.wait_ge(bcast, bcasts)
                    step(v.scalar_tensor_tensor(h[:, g, :], x[:, g, :], rstd[:, g:g + 1], mb[:, 1, g, :], ALU.mult, ALU.mult))
                    settled()
                    v.tensor_tensor(h[:, g, :], h[:, g, :], mb[:, 0, g, :], ALU.add).then_inc(h_ready, 1)

            def post_norm(q, src, bcasts):
                for g in range(NG):
                    dve.wait_ge(rstd_ready, NG * q + g + 1)
                    dve.wait_ge(bcast, bcasts)
                    step(v.scalar_tensor_tensor(h[:, g, :], src(g), rstd[:, g:g + 1], mb[:, 2, g, :], ALU.mult, ALU.mult))
                    settled()
                    v.tensor_tensor(x[:, g, :], x[:, g, :], h[:, g, :], ALU.add).then_inc(resid, 1)

            def attention(l, g):
                n = NG * l + g + 1
                K, nb = T * (1 + g), 1 + g
                cat = h[:, g, :]
                dve.wait_ge(qk_mm, n)
                v.tensor_copy(qkT[:, 4:8, :], PS[:, 1, :].rearrange("p (k t) -> p k t", k=4)).then_inc(qk_d, 1)
                dve.wait_ge(sd_mm, n)
                step(v.tensor_reduce(mx[:, :], PS[:, 3:5 + 2 * g, :].rearrange("p a (k c) -> p (a k) c", c=K), AX.X, ALU.max))
                settled()
                v.tensor_scalar(nm[:, :], mx[:, :], -DA_QK ** -0.5, None, ALU.mult).then_inc(sd_max, 1)
                if ADA_IN_ATTENTION[l][g][0] > 0:
                    finish_vector(0)
                dve.wait_ge(sd_exp, n)
                step(v.reciprocal(rr[:, :], rs[:, :]))
                settled()
                step(v.tensor_scalar(rr[:, 4:8], rr[:, 4:8], nlam[:, 0:1], None, ALU.mult))
                settled()
                for hh in range(DA_H):
                    step(v.tensor_scalar(probs[:, 4 + hh, 0:K], probs[:, 4 + hh, 0:K], rr[:, 4 + hh:5 + hh], None, ALU.mult))
                settled()
                for hh in range(DA_H):
                    last = v.scalar_tensor_tensor(comb_of(g)[:, hh, :], probs[:, hh, 0:K], rr[:, hh:hh + 1],
                                                  probs[:, 4 + hh, 0:K], ALU.mult, ALU.add)
                last.then_inc(comb_ready, 1)
                if ADA_IN_ATTENTION[l][g][0] > 1:
                    finish_vector(7)
                if g:
                    dve.wait_ge(wt_mm, n)
                    v.tensor_copy(wT[:, 4:8, :], PS[:, 1, :].rearrange("p (k t) -> p k t", k=4)).then_inc(wt_d, 1)
                dve.wait_ge(ns_mm, n)
                dve.wait_ge(comb_ready, n)
                if g == 0:
                    src = PS[:, 5:7, 0:2 * K].rearrange("p a (k c) -> p a k c", c=K)
                    step(v.tensor_reduce(mx[:, 0:4].rearrange("p (a k) -> p a k", a=2), src, AX.X, ALU.max))
                    settled()
                    v.tensor_scalar(nm[:, 0:4], mx[:, 0:4], -NA_DIM ** -0.5, None, ALU.mult).then_inc(ns_max, 1)
                else:
                    src = PS[:, 5:7, :].rearrange("p a (k c) -> p (a k) c", c=K)
                    step(v.scalar_tensor_tensor(sall[:, :, 0:T], src[:, :, 0:T], NA_DIM ** -0.5, nab[:, :, :], ALU.mult, ALU.add))
                    step(v.tensor_scalar(sall[:, :, T:K], src[:, :, T:K], NA_DIM ** -0.5, None, ALU.mult))
                    settled()
                    step(v.tensor_reduce(mx[:, 0:4], sall, AX.X, ALU.max))
                    settled()
                    v.tensor_scalar(nm[:, 0:4], mx[:, 0:4], -1.0, None, ALU.mult).then_inc(ns_max, 1)
                dve.wait_ge(oa_sq, n)
                step(v.tensor_reduce(ss[:, 4:8], sq.rearrange("p (h d) -> p h d", h=DA_H), AX.X, ALU.add))
                settled()
                v.tensor_scalar(rstd[:, 4:8], ss[:, 4:8], 1.0 / DA_V, EPS, ALU.mult, ALU.add).then_inc(oa_ms, 1)
                dve.wait_ge(pm_mm, n)
                by = "p (wh par c) -> p par wh c"
                v.tensor_tensor(cat[:, DA_W + NA_W:].rearrange(by, par=2, c=POOL_CH),
                                PS[:, 0:2, 0:2 * POOL_CH].rearrange("p a (w c) -> p a w c", c=POOL_CH),
                                pscale[:, :].rearrange(by, par=2, c=POOL_CH), ALU.mult)
                if ADA_IN_ATTENTION[l][g][1] > 0:
                    finish_vector(7)
                if g:
                    dve.wait_ge(nwt_mm, n)
                    v.tensor_copy(wT[:, 4:8, :], PS[:, 4, :].rearrange("p (k t) -> p k t", k=4)).then_inc(nwt_d, 1)
                dve.wait_ge(ns_exp, n)
                step(v.reciprocal(rr[:, 0:4], rs[:, 0:4]))
                dve.wait_ge(oa_rstd, n)
                settled()
                for hh in range(DA_H):
                    v.scalar_tensor_tensor(cat[:, hh * DA_V:(hh + 1) * DA_V], PS[:, 2, hh * DA_V:(hh + 1) * DA_V],
                                           rstd[:, 4 + hh:5 + hh], gd[:, :], ALU.mult, ALU.mult)
                dve.wait_ge(npv_mm, n)
                o = cat[:, DA_W:DA_W + NA_W].rearrange("p (k par d) -> p par k d", par=2, d=NA_DIM)
                v.tensor_tensor(o, PS[:, 5, 0:256].rearrange("p (par k d) -> p par k d", par=2, d=NA_DIM),
                                rr[:, 0:4].rearrange("p (par k) -> p par k", par=2).unsqueeze(3).to_broadcast([P, 2, 2, NA_DIM]),
                                ALU.mult).then_inc(cat_done, 1)

            dve.wait_ge(c_silu, 1)
            v.tensor_copy(cb[:, :, :, :],
                          silu_c[:, :, :].rearrange("p g j -> p j g").unsqueeze(3).to_broadcast([P, KT, NG, 16])).then_inc(c_cols, 1)
            dve.wait_ge(const_in, 16)
            v.tensor_copy(earlier[:, :], C["earlier"]).then_inc(consts16, 1)
            v.tensor_copy(ident16[:, :], ident).then_inc(consts16, 1)
            v.memset(ones[:, :], 1.0).then_inc(consts16, 1)
            for bank in range(EARLY):
                finish_vector(bank)
            for l in range(DEPTH):
                S = L[l]
                pre_norm(4 * l, BCAST * (ADA * l + 2))
                low_rows(3 * l)
                low_weights(l, "in", 0)
                lam_init = 0.8 - 0.6 * math.exp(-0.3 * l)
                dve.wait_ge(small_in, 160 * (l + 1))
                pairs = lam4[:, :, :].rearrange("p (a b) d -> p a b d", b=2)
                step(v.tensor_tensor(pairs[:, :, 0, :], pairs[:, :, 0, :], pairs[:, :, 1, :], ALU.mult))
                settled()
                v.tensor_reduce(nlam[:, 2:4], pairs[:, :, 0, :], AX.X, ALU.add).then_inc(lam_e_in, 1)
                dve.wait_ge(lam_e, l + 1)
                step(v.tensor_tensor(nlam[:, 1:2], nlam[:, 3:4], nlam[:, 2:3], ALU.subtract))
                settled()
                step(v.tensor_scalar(nlam[:, 0:1], nlam[:, 1:2], -lam_init, None, ALU.add))
                step(v.tensor_scalar(gd[:, :], gd[:, :], 1.0 - lam_init, None, ALU.mult))
                for n in range(5):
                    if n < 4:
                        low_weights(l, "in", n + 1)
                    dve.wait_ge(u_mm, 10 * l + 2 * n + 2)
                    v.tensor_copy(U[:, 1, n * HALF:(n + 1) * HALF], PS[:, (5 + 2 * n) % 8, :]).then_inc(u_d, 1)
                attention(l, 0)
                attention(l, 1)
                low_rows(3 * l + 1)
                for n in range(2):
                    low_weights(l, "out", n)
                post_norm(4 * l + 1, lambda g: PS[:, 5 - 2 * g:7 - 2 * g, :].rearrange("p a n -> p (a n)"), BCAST * (ADA * l + 3))
                pre_norm(4 * l + 2, BCAST * (ADA * l + 5))
                if ADA_AFTER_OUT[l] > 0:
                    finish_vector(7)
                rows_out(3 * l + 2)
                for g in range(NG):
                    dve.wait_ge(x_hi, NG * l + g + 1)
                    blocks = h[:, g, :].rearrange("t (p j) -> t j p", j=KT)
                    v.tensor_tensor(blocks, blocks, x3[:, g, 0, :, :], ALU.subtract).then_inc(x_rest, 1)
                for g in range(NG):
                    dve.wait_ge(x_mid, NG * l + g + 1)
                    blocks = h[:, g, :].rearrange("t (p j) -> t j p", j=KT)
                    v.tensor_tensor(x3[:, g, 2, :, :], blocks, x3[:, g, 1, :, :], ALU.subtract).then_inc(x3_ready, 1)
                for g in range(NG):
                    dve.wait_ge(sh_silu, NG * l + g + 1)
                    step(v.tensor_tensor(ssilu[:, g, :], PS[:, 4 + g, 0:F], ssilu[:, g, :], ALU.mult))
                    settled()
                    v.tensor_tensor(shid[:, g, :], PS[:, 4 + g, F:2 * F], ssilu[:, g, :], ALU.mult).then_inc(sh_hid, 1)
                dve.wait_ge(kv_out, 64 * (l + 1))
                dve.wait_ge(router_in, 32 * (l + 1))
                dve.wait_ge(s_ready, l + 1)
                step(v.tensor_tensor(sel[:, :, :], s_[:, :, :], brt[:, :].unsqueeze(1).to_broadcast([P, NG, N_EXP]), ALU.add))
                settled()
                sel8 = sel[:, :, :].rearrange("p g (a b) -> p (g a) b", b=8)
                for k in range(NG * N_EXP_GROUPS):
                    step(v.max(t8[:, k, :], sel8[:, k, :]))
                settled()
                step(v.tensor_tensor(gsc[:, :], t8[:, :, 0], t8[:, :, 1], ALU.add))
                settled()
                for g in range(NG):
                    mine = gsc[:, 8 * g:8 * g + 8].unsqueeze(2).to_broadcast([P, 8, 8])
                    others = gsc[:, 8 * g:8 * g + 8].unsqueeze(1).to_broadcast([P, 8, 8])
                    step(v.tensor_tensor(cmp1[:, :, :], others, mine, ALU.is_gt))
                    step(v.tensor_tensor(cmp2[:, :, :], others, mine, ALU.is_equal))
                    settled()
                    step(v.tensor_tensor(cmp2[:, :, :], cmp2[:, :, :], C["before"].rearrange("p (a b) -> p a b", b=8), ALU.mult))
                    settled()
                    step(v.tensor_tensor(cmp1[:, :, :], cmp1[:, :, :], cmp2[:, :, :], ALU.add))
                    settled()
                    step(v.tensor_reduce(gm[:, 8 * g:8 * g + 8], cmp1[:, :, :], AX.X, ALU.add))
                    settled()
                step(v.tensor_scalar(gm[:, :], gm[:, :], float(TOP_GROUPS), None, ALU.is_lt))
                settled()
                selm8 = selm[:, :, :].rearrange("p g (a b) -> p (g a) b", b=8)
                step(v.tensor_tensor(selm8, sel8, gm[:, :].unsqueeze(2).to_broadcast([P, 16, 8]), ALU.mult))
                step(v.tensor_scalar(gsc[:, :], gm[:, :], -1.0, BIG, ALU.add, ALU.mult))
                settled()
                step(v.tensor_tensor(selm8, selm8, gsc[:, :].unsqueeze(2).to_broadcast([P, 16, 8]), ALU.add))
                settled()
                for g in range(NG):
                    step(v.max(top8[:, g, :], selm[:, g, :]))
                settled()
                for g in range(NG):
                    step(v.match_replace(found[:, g, :], top8[:, g, :], selm[:, g, :], BIG))
                settled()
                step(v.tensor_scalar(maskf[:, :, :], found[:, :, :], BIG / 2, None, ALU.is_ge))
                settled()
                v.tensor_copy(maskb[:, :, :], maskf[:, :, :]).then_inc(mask_ready, 1)
                step(v.tensor_tensor(gates[:, :, :], maskf[:, :, :], s_[:, :, :], ALU.mult))
                settled()
                step(v.tensor_reduce(wsum[:, 0:2], gates[:, :, :], AX.X, ALU.add))
                settled()
                step(v.reciprocal(wsum[:, 2:4], wsum[:, 0:2]))
                settled()
                for g in range(NG):
                    step(v.tensor_scalar(gates[:, g, :], gates[:, g, :], wsum[:, 2 + g:3 + g], ROUTED_SCALE, ALU.mult, ALU.mult))
                for part in range(3):
                    settled()
                    step(v.tensor_copy(G3[:, :, :, part], gates[:, :, :]))
                    if part < 2:
                        settled()
                        step(v.tensor_tensor(gates[:, :, :], gates[:, :, :], G3[:, :, :, part], ALU.subtract))
                dve.wait_ge(rank_mm, l + 1)
                step(v.scalar_tensor_tensor(rk[:, :, :], PS[:, 7, 128:256].rearrange("p (g e) -> p g e", g=NG), 1000.0,
                                            maskf[:, :, :], ALU.add, ALU.mult))
                step(v.tensor_reduce(nmx[:, :], PS[:, 7, 256:320].rearrange("p (a b) -> p a b", b=2), AX.X, ALU.max))
                step(v.memset(RK[:, :, 2 * VISITS:], -1000.0))
                settled()
                for r in range(ROUNDS):
                    step(v.tensor_scalar(RK[:, :, r * N_EXP:(r + 1) * N_EXP], rk[:, :, :], -1000.0 - SLOTS * r, None, ALU.add))
                    step(v.tensor_scalar(act_[:, r * PAIRS:(r + 1) * PAIRS], nmx[:, :], SLOTS * r - 0.5, None, ALU.is_gt))
                settled()
                step(v.tensor_tensor_scan(incl[:, :], ones[:, :], act_[:, :], 0.0, ALU.mult, ALU.add))
                settled()
                step(v.tensor_tensor(pos[:, :], incl[:, :], act_[:, :], ALU.subtract))
                settled()
                step(v.scalar_tensor_tensor(pos[:, :], pos[:, :], C["row"], act_[:, :], ALU.is_equal, ALU.mult))
                step(v.tensor_scalar(item[:, 1:2], C["row"], incl[:, VISITS - 1:VISITS], float(NULL), ALU.is_ge, ALU.mult))
                settled()
                step(v.tensor_tensor(pos[:, :], pos[:, :], C["visit"], ALU.mult))
                settled()
                step(v.tensor_reduce(item[:, 2:3], pos[:, :], AX.X, ALU.add))
                settled()
                v.tensor_tensor(item[:, 0:1], item[:, 1:2], item[:, 2:3], ALU.add).then_inc(item_ready, 1)
                step(v.tensor_scalar(n_visits[0:1, 0:1], incl[0:1, VISITS - 1:VISITS], 1.0, None, ALU.add))
                settled()
                step(v.tensor_scalar(n_visits[0:1, 0:1], n_visits[0:1, 0:1], 1, 1, ALU.logical_shift_right, ALU.logical_shift_left))
                step(v.memset(visits[0:1, VISITS:], NULL))
                step(v.memset(yhi[:, :].bitcast(f32), 0.0))
                step(v.memset(put[:, 1, :].bitcast(f32), 0.0))
                step(v.memset(slot_gate[:, :], 0.0))
                settled()
                for n in range(2):
                    v.memset(ylo[:, n * HALF:(n + 1) * HALF].bitcast(f32), 0.0).then_inc(S["ylo_done"], 1)
                dve.wait_ge(item_mm, l + 1)
                step(v.tensor_copy(visits[0:1, 0:VISITS], PS[0:1, 7, 320:448]))
                dve.wait_ge(shd_mm, l + 1)
                settled()
                v.sem_inc(table_ready, 1)

                def choose(u, visit):
                    slots = RK[:, :, bass.ds(visit * 2, 2)].unsqueeze(3).to_broadcast([P, NG, 2, SLOTS])
                    iota = C["slot"].unsqueeze(1).unsqueeze(1).to_broadcast([P, NG, 2, SLOTS])
                    v.tensor_tensor(pick[:, u % 2, :, 0:P].rearrange("p g (e s) -> p g e s", e=2), iota, slots, ALU.is_equal)
                    pair = visit & (PAIRS - 1)
                    v.tensor_copy(pick[:, u % 2, :, P:P + 6],
                                  G3[:, :, :, :].rearrange("p g e k -> p g (e k)")[:, :, bass.ds(pair * 6, 6)]).then_inc(S["picked"], 1)

                def slots_of(u):
                    v.tensor_copy(put[:, u % 2, :].rearrange("p (g t) -> p g t", g=NG),
                                  PS[:, 6, 0:128].rearrange("p (g t) -> p g t", g=NG).bitcast(bf16))
                    for e in range(2):
                        last = v.tensor_reduce(slot_gate[64 * e:64 * e + 64, u % 2:u % 2 + 1],
                                               PS[64 * e:64 * e + 64, 6, 128 + 3 * e:131 + 3 * e], AX.X, ALU.add)
                    last.then_inc(S["slots_done"], 1)

                count = dve.value_load(n_visits[0:1, 0:1], min_val=PAIRS, max_val=VISITS)
                choose(0, 0)
                choose(1, 1)
                dve.wait_ge(S["put_mm"], 1)
                slots_of(0)
                dve.wait_ge(S["ga_mm"], 2)
                v.tensor_copy(xgT[:, 0, 4:8, :], PS[:, 5, :].rearrange("p (j s) -> p j s", j=4)).then_inc(S["xg_d"], 1)
                with dve.Fori(0, count, 2) as i:
                    for b in range(2):
                        visit = dve.value_load(visits[0:1, bass.ds(i + (b + 2), 1)], min_val=0, max_val=NULL)
                        dve.wait_ge(S["ga_mm"], i * 2 + (2 * b + 4))
                        v.tensor_copy(xgT[:, 1 - b, 4:8, :], PS[:, 5, :].rearrange("p (j s) -> p j s", j=4)).then_inc(S["xg_d"], 1)
                        dve.wait_ge(S["silu_done"], i + (b + 1))
                        dve.wait_ge(S["slots_done"], i + (b + 1))
                        v.scalar_tensor_tensor(hid[:, :], PS[:, 4, F:2 * F], slot_gate[:, b:b + 1], silu[:, :], ALU.mult, ALU.mult)\
                            .then_inc(S["hid_done"], 1)
                        dve.wait_ge(S["put_mm"], i + (b + 2))
                        slots_of(b + 1)
                        choose(b, visit)
                        for n, bank in enumerate((6, 4)):
                            dve.wait_ge(S["yhi_done"], i * 2 + (2 * b + n + 1))
                            cols = slice(n * HALF, (n + 1) * HALF)
                            v.tensor_tensor(ylo[:, cols], PS[:, bank, :], yhi[:, cols].bitcast(f32), ALU.subtract).then_inc(S["ylo_done"], 1)
                post_norm(4 * l + 3, lambda g: PS[:, 2 * g:2 * g + 2, :].rearrange("p a n -> p (a n)"), BCAST * ADA * (l + 1))


OUTPUTS = (("y_prompt", (1, T, D)), ("y_sample", (1, T, D)), ("new_diff_k", (1, DEPTH, T, DA_H, 2 * DA_QK)),
           ("new_diff_v", (1, DEPTH, T, DA_H, DA_V)), ("new_na_k", (1, DEPTH, T, NA_H, NA_DIM)),
           ("new_na_v", (1, DEPTH, T, NA_H, NA_DIM)))
PASSED = ("x_prompt", "x_sample", "cache_diff_k", "cache_diff_v", "cache_na_k", "cache_na_v", "c", "c_ctx", "w_ada",
          "w_in", "w_out", "diff_lambda", "g_diff", "pool_w", "pool_scale", "w_router", "b_router",
          "w_gate", "w_up", "w_down", "ws_gate", "ws_up", "ws_down")


def constants():
    where, n = const_layout()
    out = np.zeros((P, n), np.float32)

    def put(name, a):
        at, m = where[name]
        out[:, at:at + m] = np.asarray(a, np.float32).reshape(P, m)
    t = np.arange(T)
    put("ident", np.eye(P))
    nf = DA_QK // 4
    pos = np.stack([t // GRID_W, t % GRID_W], -1).astype(np.float32)
    ang = pos[:, :, None] * np.power(np.float32(10000.0), -np.arange(nf, dtype=np.float32) / nf)
    put("cos", np.repeat(np.cos(ang)[:, :, None, :], 2, 2))
    put("sin", np.sin(ang))
    bands = []
    for w in WINDOWS:
        lo, hi = np.clip(t - w // 2, 0, T), np.clip(t + w // 2, 0, T)
        m = (t[:, None] >= lo) & (t[:, None] < hi)
        bands.append(m / (hi - lo) - np.eye(T))
    put("band", np.stack(bands, 1))
    put("before", np.broadcast_to(np.arange(8)[None, :] < np.arange(8)[:, None], (P, 8, 8)))
    put("slot", np.broadcast_to(np.arange(SLOTS), (P, SLOTS)))
    put("row", np.arange(P))
    put("visit", np.broadcast_to(np.arange(VISITS), (P, VISITS)))
    put("minus_half", np.full((P, 4), -0.5))
    put("earlier", t[:, None] < t[None, :])
    return out


def bias_grid(na_bias):
    t = np.arange(T)
    r, c = t // GRID_W, t % GRID_W
    start = np.clip(c - NA_COLS // 2, 0, GRID_W - NA_COLS)
    inside = (c[None, :] >= start[:, None]) & (c[None, :] < start[:, None] + NA_COLS)
    off_r = r[None, :] - r[:, None] + NA_ROWS - 1
    off_c = np.clip(c[None, :] - c[:, None] + NA_COLS - 1, 0, 2 * NA_COLS - 2)
    grid = na_bias[:, :, off_r, off_c]
    grid = np.where(inside, grid, np.float32(NEG))[:, [0, 2, 1, 3]]
    return np.ascontiguousarray(grid.transpose(0, 2, 1, 3))


def kernel(**inputs):
    import concourse.bacc as bacc
    from concourse.bass_utils import run_bass_kernel_spmd

    a = {k: np.asarray(x) for k, x in inputs.items()}
    arrays = {k: np.ascontiguousarray(a[k]) for k in PASSED}
    arrays["const"] = constants()
    arrays["na_bias_grid"] = bias_grid(a["na_bias"])
    bias = a["b_ada"].reshape(DEPTH, ADA, D)
    gain = bias.copy()
    for i, name in ((1, "g_pre_mix"), (2, "g_post_mix"), (4, "g_pre_ffn"), (5, "g_post_ffn")):
        gain[:, i] = a[name]
    vec_rows = np.zeros((4, NG, 16, 2, QUARTER), bias.dtype)
    for k, rows in enumerate((bias, gain)):
        vec_rows[:, :, 0:DEPTH * ADA, k] = rows.reshape(DEPTH * ADA, 4, QUARTER).transpose(1, 0, 2)[:, None]
    arrays["vec_rows"] = vec_rows.reshape(P, 2, QUARTER)
    nc = bacc.Bacc("TRN2", target_bir_lowering=False, num_devices=1)
    io = {k: nc.dram_tensor(f"in_{k}", v.shape, mybir.dt.from_np(v.dtype), kind="ExternalInput").ap() for k, v in arrays.items()}
    for name, shape in OUTPUTS:
        io[name] = nc.dram_tensor(f"out_{name}", shape, mybir.dt.float32, kind="ExternalOutput").ap()
    program(nc, io)
    r = run_bass_kernel_spmd(nc, [{f"in_{k}": v for k, v in arrays.items()}], core_ids=[0])
    return tuple(r.results[0][f"out_{name}"] for name, _ in OUTPUTS)
```
